# Optimizing a Trainium2 kernel written in Bass

```python
import jax, jax.numpy as jnp
from jax import lax
import numpy as np

D_MODEL = 1024
BATCH = 1
SEQ = 2048
DEPTH = 1

CONV_CH = D_MODEL // 2
N_CONV_GROUPS = 8
HEAD_DIM = 64
N_HEADS = (D_MODEL // 2) // HEAD_DIM
ATTN_W = N_HEADS * HEAD_DIM
MIX_W = CONV_CH + ATTN_W
CONV_K = 3
D_FF = ((8 * D_MODEL) // 3 + 255) // 256 * 256
Q_BLOCK = 128
EPS = 1e-6
FORGET_BIAS_INIT = 3.0
IN_COLS = 3 * CONV_CH + 3 * ATTN_W + N_HEADS

kernel_name = "hymba_conv_fox_convffn_layer"

def rmsnorm(x, g):
    xf = x.astype(jnp.float32)
    y = xf * lax.rsqrt(jnp.mean(xf * xf, axis=-1, keepdims=True) + EPS)
    return (y * g.astype(jnp.float32)).astype(x.dtype)

def causal_dwconv(x, w):
    s = x.shape[1]
    xp = jnp.pad(x, ((0, 0), (CONV_K - 1, 0), (0, 0)))
    return sum(xp[:, j:j + s, :] * w[j] for j in range(CONV_K))

def fox_attention(q, k, v, log_f):
    b, s, h, dh = q.shape
    nblk = s // Q_BLOCK
    scale = 1.0 / np.sqrt(dh).astype(np.float32)
    F = jnp.transpose(jnp.cumsum(log_f, axis=1), (0, 2, 1))
    q_blocks = jnp.transpose(q.reshape(b, nblk, Q_BLOCK, h, dh), (1, 0, 2, 3, 4))
    f_blocks = jnp.transpose(F.reshape(b, h, nblk, Q_BLOCK), (2, 0, 1, 3))
    kpos = jnp.arange(s)

    def one_block(args):
        qb, fqb, i = args
        qpos = i * Q_BLOCK + jnp.arange(Q_BLOCK)
        sc = jnp.einsum('bqhd,bkhd->bhqk', qb, k,
                        preferred_element_type=jnp.float32) * scale
        logits = sc + fqb[..., None] - F[:, :, None, :]
        mask = kpos[None, :] <= qpos[:, None]
        logits = jnp.where(mask[None, None], logits, -jnp.inf)
        p = jax.nn.softmax(logits, axis=-1)
        return jnp.einsum('bhqk,bkhd->bqhd', p.astype(v.dtype), v)

    out = lax.map(one_block, (q_blocks, f_blocks, jnp.arange(nblk)))
    return jnp.transpose(out, (1, 0, 2, 3, 4)).reshape(b, s, h * dh)

def setup_inputs(seed: int = 0) -> dict:
    key = jax.random.key(seed)
    ks = jax.random.split(key, 16)
    nrm = lambda k, shape, sc: jax.random.normal(k, shape, jnp.float32) * sc
    gain = lambda k, shape: 1.0 + 0.02 * jax.random.normal(k, shape, jnp.float32)
    return {
        "x": jax.random.normal(ks[0], (BATCH, SEQ, D_MODEL), jnp.float32),
        "g_mix": gain(ks[1], (DEPTH, D_MODEL)),
        "w_in": nrm(ks[2], (DEPTH, D_MODEL, IN_COLS), D_MODEL ** -0.5),
        "b_f": FORGET_BIAS_INIT + 0.1 * jax.random.normal(ks[3], (DEPTH, N_HEADS), jnp.float32),
        "w_conv": nrm(ks[4], (DEPTH, CONV_K, CONV_CH), CONV_K ** -0.5),
        "g_conv_out": gain(ks[5], (DEPTH, CONV_CH)),
        "g_attn_out": gain(ks[6], (DEPTH, ATTN_W)),
        "w_o": nrm(ks[7], (DEPTH, MIX_W, D_MODEL), MIX_W ** -0.5),
        "g_ffn": gain(ks[8], (DEPTH, D_MODEL)),
        "w_up": nrm(ks[9], (DEPTH, D_MODEL, 2 * D_FF), D_MODEL ** -0.5),
        "w_ffn_conv": nrm(ks[10], (DEPTH, CONV_K, 2 * D_FF), CONV_K ** -0.5),
        "w_down": nrm(ks[11], (DEPTH, D_FF, D_MODEL), D_FF ** -0.5),
        "g_final": gain(ks[12], (D_MODEL,)),
    }

def reference(x, g_mix, w_in, b_f, w_conv, g_conv_out, g_attn_out, w_o,
              g_ffn, w_up, w_ffn_conv, w_down, g_final):
    b, s, _ = x.shape
    o1 = CONV_CH
    o2 = 2 * CONV_CH
    o3 = 3 * CONV_CH
    o4 = o3 + ATTN_W
    o5 = o4 + ATTN_W
    o6 = o5 + ATTN_W
    for l in range(DEPTH):
        h = rmsnorm(x, g_mix[l])
        z = h @ w_in[l]
        gb, gc, xc = z[..., :o1], z[..., o1:o2], z[..., o2:o3]
        q = z[..., o3:o4].reshape(b, s, N_HEADS, HEAD_DIM)
        k = z[..., o4:o5].reshape(b, s, N_HEADS, HEAD_DIM)
        v = z[..., o5:o6].reshape(b, s, N_HEADS, HEAD_DIM)
        f_logit = z[..., o6:]
        y_conv = gb * causal_dwconv(gc * xc, w_conv[l])
        log_f = jax.nn.log_sigmoid((f_logit + b_f[l]).astype(jnp.float32))
        y_attn = fox_attention(q, k, v, log_f)
        mix = jnp.concatenate([rmsnorm(y_conv, g_conv_out[l]),
                               rmsnorm(y_attn, g_attn_out[l])], axis=-1)
        x = x + mix @ w_o[l]
        h = rmsnorm(x, g_ffn[l])
        u = causal_dwconv(h @ w_up[l], w_ffn_conv[l])
        a, g = u[..., :D_FF], u[..., D_FF:]
        x = x + (jax.nn.silu(g) * a) @ w_down[l]
    return rmsnorm(x, g_final)


_drawn_inputs = setup_inputs


def setup_inputs(seed=0):
    import zlib

    import numpy as np

    out = dict(_drawn_inputs(seed))
    spreads = {}
    factors = {'g_conv_out': 5.112, 'g_attn_out': 5.066, 'g_ffn': 5.248, 'g_final': 2.889}
    for name, (base, spread) in spreads.items():
        noise = np.random.default_rng([zlib.crc32(name.encode()), seed]).standard_normal(out[name].shape)
        drawn = base * np.exp(spread * noise) if base else spread * noise
        out[name] = __import__('jax').numpy.asarray(drawn.astype(out[name].dtype))
    for name, factor in factors.items():
        out[name] = (out[name] * factor).astype(out[name].dtype)
    return out
```

```python
from contextlib import ExitStack

import concourse.bass as bass
from concourse import mybir

F32 = mybir.dt.float32
F32R = mybir.dt.float32r
BF16 = mybir.dt.bfloat16
ALU = mybir.AluOpType
ACT = mybir.ActivationFunctionType
AX = mybir.AxisListType

P = 128
BANK = 512
DMA = 16
EPS = 1e-6


class Sizes:

    def __init__(self, x, w_in, w_conv, g_attn_out, b_f, w_up, w_down):
        _, self.seq, self.d = x.shape
        self.conv = w_conv.shape[-1]
        self.attn = g_attn_out.shape[-1]
        self.heads = b_f.shape[-1]
        self.hd = self.attn // self.heads
        self.ff = w_down.shape[-2]
        self.taps = w_conv.shape[-2]
        self.dc = self.d // P
        self.tiles = self.seq // P
        self.blocks = self.seq // BANK
        assert self.hd == 64 and self.taps == 3 and self.conv == self.attn == 512
        assert w_in.shape[-1] == 3 * self.conv + 3 * self.attn + self.heads
        assert w_up.shape[-1] == 2 * self.ff


class Memory:

    def __init__(self, nc, ctx):
        self.nc, self.ctx = nc, ctx

    def sb(self, name, shape, dt=F32):
        return self.ctx.enter_context(self.nc.sbuf_tensor(name, shape, dt))

    def ps(self, name, shape, dt=F32):
        return self.ctx.enter_context(self.nc.psum_tensor(name, shape, dt))

    def sem(self, name):
        return self.ctx.enter_context(self.nc.semaphore(name))


def split_product(nc, out, pairs, start, stop):
    last = None
    for n, (l_hi, l_lo, r_hi, r_lo) in enumerate(pairs):
        nc.tensor.matmul(out, l_hi, r_hi, start=start and n == 0, stop=False)
        nc.tensor.matmul(out, l_hi, r_lo, start=False, stop=False)
        last = nc.tensor.matmul(out, l_lo, r_hi, start=False, stop=stop and n == len(pairs) - 1)
    return last


def project_inputs(nc, z, k, a, d):
    C, B, T, H = z.dc, z.blocks, z.tiles, z.heads
    TB = BANK // P
    x_v = a["x"][0].rearrange("(b j p) d -> b p j d", j=TB, p=P)
    w_v = a["w_in"][0].rearrange("(c p) n -> p c n", p=P)
    conv_cols = [z.conv, 2 * z.conv, 0]
    qkv_cols = [3 * z.conv + n * z.attn for n in range(3)]
    gate_cols = 3 * z.conv + 3 * z.attn
    mix_v, qkv_v = d["mix"], d["qkv"]

    with ExitStack() as ctx:
        m = Memory(nc, ctx)
        hT_hi = m.sb("hT_hi", [P, C, z.seq], F32R)
        hT_lo = m.sb("hT_lo", [P, C, z.seq], F32R)
        w_raw = m.sb("w_raw", [P, C, P])
        w_hi = m.sb("w_hi", [P, 3, C, P], F32R)
        w_lo = m.sb("w_lo", [P, 3, C, P], F32R)
        g_mix = m.sb("g_mix", [P, C])
        w_conv = m.sb("w_conv_sb", [P, z.taps, z.conv // P])
        ssq = m.sb("ssq_x", [P, 2, TB])
        rms = m.sb("rms_x", [P, 2, TB])
        rstd = m.sb("rstd_x", [P, 2, TB])
        gate_raw = m.sb("gate_raw", [P, C, H])
        gate_bias = m.sb("gate_bias", [2 * H, 1])
        pair_sum = m.sb("pair_sum", [2 * H, H])
        gT = m.sb("gT", [2 * H, 2, BANK])
        gate = [m.sb(f"gate{n}", [P, H, T]) for n in range(3)]
        run = [m.sb(f"run{n}", [P, H, T]) for n in range(2)]
        fcum = m.sb("fcum", [P, H, T])
        f_parts = m.sb("f_parts", [P, 4, T * H], F32R)
        tri = m.sb("tri", [P, P])
        ones = m.sb("ones_f", [P, P])

        rows = m.sb("rows", [P, 4, P])
        conv_rms = m.sb("conv_rms", [P, T])

        psum = m.ps("psum_a", [P, 8, BANK])
        xT_ps = [psum[:, 0, :], psum[:, 1, :]]
        logit_ps = psum[:, 2, 0:T * H].rearrange("p (h t) -> p h t", h=H)
        gate_ps = psum[:, 3, :]
        z_ps = [psum[:, 4 + n, :] for n in range(B)]

        consts_built = m.sem("consts_built")
        vectors_loaded = m.sem("vectors_loaded")
        ffn_conv_loaded = m.sem("ffn_conv_loaded")
        gate_w_loaded = m.sem("gate_w_loaded")
        x_loaded = [[m.sem(f"x_loaded{u}{j}") for j in range(TB)] for u in range(2)]
        x_squared = m.sem("x_squared")
        rms_ready = m.sem("rms_ready")
        rstd_ready = m.sem("rstd_ready")
        x_normed = m.sem("x_normed")
        xT_ready = m.sem("xT_ready")
        hT_hi_ready = m.sem("hT_hi_ready")
        hT_lo_ready = m.sem("hT_lo_ready")
        gate_w_ready = m.sem("gate_w_ready")
        gT_ready = m.sem("gT_ready")
        logits_turned = m.sem("logits_turned")
        gate_act = m.sem("gate_act")
        gate_dve = m.sem("gate_dve")
        cum_ready = m.sem("cum_ready")
        rows_turned = m.sem("rows_turned")
        rows_ready = m.sem("rows_ready")
        rows_stored = m.sem("rows_stored")
        w_loaded = m.sem("w_loaded")
        w_hi_ready = m.sem("w_hi_ready")
        w_split = m.sem("w_split")
        projected = m.sem("projected")
        gc_ready = m.sem("gc_ready")
        evacuated = m.sem("evacuated")
        conv_step = m.sem("conv_step")
        y_squared = m.sem("y_squared")
        sq_summed = m.sem("sq_summed")
        out_stored = [m.sem(f"out_stored{b}") for b in range(B)]
        sums_ready = m.sem("sums_ready")
        conv_rms_ready = m.sem("conv_rms_ready")

        early = ExitStack()
        xb = early.enter_context(nc.sbuf_tensor("xb", [P, 2, TB, z.d], F32))
        junk = early.enter_context(nc.sbuf_tensor("junk", [P, z.d], BF16))
        early.close()
        gc_sb = m.sb("gc_sb", [P, z.seq])
        prod = m.sb("prod", [P, 2 + z.seq])
        y_sb = m.sb("y_sb", [P, B, BANK])
        y_sq = m.sb("y_sq", [P, BANK])
        sq_sum = m.sb("sq_sum", [P, z.seq])

        CT = z.conv // P
        CONV_DONE = B + 2 * B * CT

        def at_block(t, n):
            return t[:, n * BANK:(n + 1) * BANK]

        ctx.enter_context(nc.allow_non_contiguous_dma(reason="small vectors, a channel per partition"))
        block = ctx.enter_context(nc.Block())

        @block.sync
        def _(sp):
            sp.dma_start(g_mix[:, :], a["g_mix"][0].rearrange("(c p) -> p c", p=P)).then_inc(vectors_loaded, DMA)
            sp.dma_start(w_conv[:, :, :], a["w_conv"][0].rearrange("j (c p) -> p j c", p=P)) \
                .then_inc(vectors_loaded, DMA)
            sp.dma_start(gate_raw[:, :, :], w_v[:, :, gate_cols:gate_cols + H]).then_inc(gate_w_loaded, DMA)
            sp.wait_ge(consts_built, 1)
            sp.dma_start(gate_bias[0:H, :], a["b_f"].rearrange("o h -> h o")).then_inc(vectors_loaded, DMA)
            with sp.Fori(0, B // 2) as i:
                for u in range(2):
                    sp.wait_ge(xT_ready, 2 * C * i + C * (u + 1))
                    for j in range(TB):
                        sp.dma_start(xb[:, u, j, :],
                                     x_v[bass.ds(2 * i + u, 1), :, j, :].rearrange("o p d -> (o p) d")) \
                            .then_inc(x_loaded[u][j], DMA)
            sp.dma_start(k["w_ffn_conv"][:, :, :], a["w_ffn_conv"][0].rearrange("j (c p) -> p j c", p=P)) \
                .then_inc(ffn_conv_loaded, DMA)
            for base, cols in ((0, conv_cols), (3 * CT, qkv_cols)):
                with sp.Fori(1, CT + 1) as i:
                    for t in range(3):
                        sp.wait_ge(w_split, 3 * i + (base + t - 2))
                        sp.dma_start(w_raw[:, :, :], w_v[:, :, bass.ds(P * i + (cols[t] - P), P)]) \
                            .then_inc(w_loaded, DMA)
            sp.wait_ge(rows_ready, 1)
            sp.dma_start(d["gate_rows"].rearrange("r h (b t) -> (h b) r t", t=P), rows[:, :, :]) \
                .then_inc(rows_stored, DMA)
            sp.wait_ge(rows_stored, DMA)
            sp.wait_ge(ffn_conv_loaded, DMA)
            for b in range(B):
                sp.wait_ge(out_stored[b], DMA * (1 + CT + 3 * CT))

        @block.gpsimd
        def _(pool):
            g = nc.gpsimd
            ident, ident_bf, causal, fold = k["ident"], k["ident_bf"], k["causal"], k["fold"]
            for t, v in ((ident, 0.0), (ident_bf, 0.0), (causal, 0.0), (fold, 0.0), (pair_sum, 0.0), (tri, 1.0),
                         (ones, 1.0), (k["eps"], EPS), (k["zero"], 0.0)):
                g.memset(t[:, :], v)
            g.memset(w_lo[:, 2, :, :].bitcast(F32), 0.0)
            g.memset(gate_bias[:, :], 0.0).then_inc(consts_built, 1)
            pool.wait_ge(consts_built, 1)
            for t in (ident, ident_bf):
                g.affine_select(out=t[:, :], in_=t[:, :], compare_op=ALU.not_equal, fill=1.0, base=0,
                                pattern=[[-1, P]], channel_multiplier=1)
            g.affine_select(out=causal[:, :], in_=causal[:, :], compare_op=ALU.is_ge, fill=-1e30, base=0,
                            pattern=[[-1, P]], channel_multiplier=1)
            g.affine_select(out=tri[:, :], in_=tri[:, :], compare_op=ALU.is_ge, fill=0.0, base=0,
                            pattern=[[1, P]], channel_multiplier=-1)
            for part in range(2):
                g.affine_select(out=fold[:, :], in_=fold[:, :], compare_op=ALU.not_equal, fill=1.0,
                                base=-z.hd * part, pattern=[[-1, z.hd]], channel_multiplier=1)
                g.affine_select(out=pair_sum[:, :], in_=pair_sum[:, :], compare_op=ALU.not_equal, fill=1.0,
                                base=-H * part, pattern=[[-1, H]], channel_multiplier=1).then_inc(consts_built, 1)
                pool.wait_ge(consts_built, part + 2)
            pool.wait_ge(gate_w_loaded, DMA)
            g.tensor_copy(w_lo[:, 2, :, 0:H], gate_raw[:, :, :]).then_inc(gate_w_ready, 1)
            pool.wait_ge(gate_w_ready, 1)
            g.tensor_tensor(w_lo[:, 2, :, H:2 * H], gate_raw[:, :, :], w_lo[:, 2, :, 0:H].bitcast(F32),
                            ALU.subtract).then_inc(gate_w_ready, 1)
            zero = k["zero"][:, :].unsqueeze(2).broadcast_to([P, C, P])
            pool.sem_inc(w_split, 1)
            for base in (0, 3 * CT):
                with pool.Fori(0, CT) as i:
                    for t in range(3):
                        n = base + t
                        pool.wait_ge(w_loaded, 3 * DMA * i + DMA * (n + 1))
                        pool.wait_ge(projected, 3 * B * i + B * (n + 1))
                        g.tensor_tensor(w_hi[:, t, :, :], w_raw[:, :, :], zero, ALU.add).then_inc(w_hi_ready, 1)
                        pool.wait_ge(w_hi_ready, 3 * i + (n + 1))
                        g.tensor_tensor(w_lo[:, t, :, :], w_raw[:, :, :], w_hi[:, t, :, :].bitcast(F32),
                                        ALU.subtract).then_inc(w_split, 1)

        @block.tensor
        def _(pe):
            ident = k["ident"]
            pe.sem_inc(xT_ready, 2 * C)
            pe.sem_inc(projected, 2 * B)
            pe.wait_ge(consts_built, 3)
            pe.wait_ge(gate_w_ready, 2)
            with pe.Fori(0, B // 2) as i:
                for u in range(2):
                    pe.wait_ge(x_normed, 2 * TB * i + TB * (u + 1))
                    for c in range(C):
                        pe.wait_ge(hT_lo_ready, 2 * C * i + (C * u + c + 1))
                        for j in range(TB):
                            last = nc.tensor.transpose(xT_ps[c % 2][:, j * P:(j + 1) * P],
                                                       xb[:, u, j, c * P:(c + 1) * P], ident[:, :])
                        last.then_inc(xT_ready, 1)
                    pe.wait_ge(hT_lo_ready, 2 * C * i + (C * u + C + 2))
                    pe.wait_ge(gT_ready, 2 * i + (u + 1))
                    for c in range(C):
                        at = bass.ds(2 * BANK * i + u * BANK, BANK)
                        nc.tensor.matmul(gate_ps, w_lo[:, 2, c, :], hT_hi[:, c, at], start=c == 0, stop=False)
                        last = nc.tensor.matmul(gate_ps, w_lo[:, 2, c, :], hT_lo[:, c, at], start=False,
                                                stop=c == C - 1)
                    last.then_inc(projected, 1)
                    pe.wait_ge(gT_ready, 2 * i + (u + 2))
                    for j in range(TB):
                        last = nc.tensor.matmul(logit_ps[:, :, bass.ds(2 * TB * i + (TB * u + j), 1)]
                                                .rearrange("p h o -> p (h o)"),
                                                gT[:, u, j * P:(j + 1) * P], pair_sum[:, :], start=True, stop=True)
                    last.then_inc(logits_turned, 1)

            def tile(n, t, bank_is_free):
                pe.wait_ge(w_split, n + 2)
                for b in range(B):
                    bank_is_free(b)
                    split_product(nc, z_ps[b], [(w_hi[:, t, c, :], w_lo[:, t, c, :],
                                                 at_block(hT_hi[:, c, :], b), at_block(hT_lo[:, c, :], b))
                                                for c in range(C)], True, True).then_inc(projected, 1)

            with pe.Fori(0, CT) as i:
                tile(3 * i, 0, lambda b: pe.wait_ge(evacuated, 2 * B * i + (b + 1)))
                tile(3 * i + 1, 1, lambda b: pe.wait_ge(gc_ready, B * i + (b + 1)))
                tile(3 * i + 2, 2, lambda b: pe.wait_ge(evacuated, 2 * B * i + (B + b + 1)))
            pe.wait_ge(gate_dve, 1)
            nc.tensor.matmul(psum[:, 2, 0:T * H], tri[:, :], gate[0][:, :, :].rearrange("p h t -> p (h t)"),
                             start=True, stop=True)
            nc.tensor.matmul(psum[:, 3, 0:T * H], ones[:, :], gate[0][:, :, :].rearrange("p h t -> p (h t)"),
                             start=True, stop=True).then_inc(cum_ready, 1)
            with pe.Fori(0, CT) as i:
                for t in range(3):
                    tile(3 * i + (3 * CT + t), t,
                         lambda b: pe.wait_ge(evacuated, 3 * B * i + (CONV_DONE - B + B * t + b + 1)))
            pe.wait_ge(gate_act, 6)
            pe.wait_ge(gate_dve, 13)
            for n in range(4):
                last = nc.tensor.transpose(xT_ps[0][:, n * P:(n + 1) * P], f_parts[:, n, :].bitcast(F32), ident[:, :])
            last.then_inc(rows_turned, 1)
            pe.wait_ge(sq_summed, 1 + B * CT)
            for t in range(T):
                last = nc.tensor.matmul(gate_ps[:, t:t + 1], sq_sum[:, t * P:(t + 1) * P], ones[:, 0:1],
                                        start=True, stop=True)
            last.then_inc(sums_ready, 1)

        @block.scalar
        def _(act):
            act.sem_inc(x_squared, 1)
            act.sem_inc(gT_ready, 1)
            for b in range(B):
                act.sem_inc(out_stored[b], DMA)
            act.wait_ge(vectors_loaded, 3 * DMA)
            act.wait_ge(consts_built, 1)
            with act.Fori(0, B // 2) as i:
                for u in range(2):
                    for j in range(TB):
                        act.wait_ge(x_loaded[u][j], DMA * i + DMA)
                        act.wait_ge(x_squared, 2 * TB * i + (TB * u + j + 1))
                        nc.scalar.activation(junk[:, :], xb[:, u, j, :], ACT.Square,
                                             accum_out=ssq[:, u, j:j + 1]).then_inc(x_squared, 1)
                    act.wait_ge(x_squared, 2 * TB * i + (TB * (u + 1) + 1))
                    nc.scalar.activation(rms[:, u, :], ssq[:, u, :], ACT.Sqrt, bias=k["eps"][:, :],
                                         scale=1.0 / z.d).then_inc(rms_ready, 1)
                    for c in range(C):
                        act.wait_ge(xT_ready, 2 * C * i + (2 * C + C * u + c + 1))
                        nc.scalar.activation(hT_hi[:, c, bass.ds(2 * BANK * i + u * BANK, BANK)], xT_ps[c % 2],
                                             ACT.Copy, scale=g_mix[:, c:c + 1]).then_inc(hT_hi_ready, 1)
                    act.wait_ge(projected, 2 * i + (2 * B + u + 1))
                    nc.scalar.activation(gT[:, u, :], gate_ps[0:2 * H, :], ACT.Identity,
                                         bias=gate_bias[:, :]).then_inc(gT_ready, 1)
            act.wait_ge(logits_turned, B)
            nc.scalar.activation(gate[0][:, :, :], logit_ps, ACT.Copy).then_inc(gate_act, 1)
            act.wait_ge(gate_act, 1)
            nc.scalar.activation(gate[1][:, :, :], gate[0][:, :, :], ACT.Abs).then_inc(gate_act, 1)
            act.wait_ge(gate_act, 2)
            nc.scalar.activation(gate[2][:, :, :], gate[1][:, :, :], ACT.Exp, scale=-1.0).then_inc(gate_act, 1)
            act.wait_ge(gate_act, 3)
            nc.scalar.activation(gate[1][:, :, :], gate[2][:, :, :], ACT.Ln, bias=1.0).then_inc(gate_act, 1)
            with act.Fori(0, CT) as i:
                for b in range(B):
                    act.wait_ge(projected, 3 * B * i + (3 * B + b + 1))
                    nc.scalar.activation(at_block(gc_sb, b), z_ps[b], ACT.Copy).then_inc(gc_ready, 1)
                for b in range(B):
                    act.wait_ge(evacuated, 2 * B * i + (2 * B + b + 1))
                    act.wait_ge(sq_summed, B * i + (b + 1))
                    nc.scalar.activation(y_sq[:, :], y_sb[:, b, :], ACT.Square).then_inc(y_squared, 1)
                    act.dma_start(mix_v[bass.ds(P * i, P), b * BANK:(b + 1) * BANK], y_sb[:, b, :]) \
                        .then_inc(out_stored[b], DMA)
            act.wait_ge(gate_dve, 11)
            nc.scalar.activation(f_parts[:, 0, :], fcum[:, :, :].rearrange("p h t -> p (h t)"), ACT.Copy,
                                 scale=-1.0).then_inc(gate_act, 1)
            nc.scalar.activation(f_parts[:, 2, :], fcum[:, :, :].rearrange("p h t -> p (h t)"),
                                 ACT.Copy).then_inc(gate_act, 1)
            with act.Fori(0, CT) as i:
                for t in range(3):
                    for b in range(B):
                        act.wait_ge(evacuated, 3 * B * i + (CONV_DONE + B * t + b + 1))
                        act.dma_start(qkv_v[t, bass.ds(P * i, P), b * BANK:(b + 1) * BANK], y_sb[:, b, :]) \
                            .then_inc(out_stored[b], DMA)
            act.wait_ge(sums_ready, 1)
            nc.scalar.activation(conv_rms[:, :], gate_ps[:, 0:T], ACT.Sqrt, bias=k["eps"][:, :],
                                 scale=1.0 / z.conv).then_inc(conv_rms_ready, 1)

        @block.vector
        def _(dve):
            v = nc.vector
            dve.sem_inc(hT_lo_ready, 2)
            dve.sem_inc(evacuated, B)
            dve.sem_inc(sq_summed, 1)
            with dve.Fori(0, B // 2) as i:
                for u in range(2):
                    dve.wait_ge(rms_ready, 2 * i + (u + 1))
                    v.reciprocal(rstd[:, u, :], rms[:, u, :]).then_inc(rstd_ready, 1)
                    dve.wait_ge(rstd_ready, 2 * i + (u + 1))
                    for j in range(TB):
                        v.tensor_scalar(xb[:, u, j, :], xb[:, u, j, :], rstd[:, u, j:j + 1], None,
                                        ALU.mult).then_inc(x_normed, 1)
                    for c in range(C):
                        dve.wait_ge(hT_hi_ready, 2 * C * i + (C * u + c + 1))
                        at = bass.ds(2 * BANK * i + u * BANK, BANK)
                        v.scalar_tensor_tensor(hT_lo[:, c, at], xT_ps[c % 2], g_mix[:, c:c + 1],
                                               hT_hi[:, c, at].bitcast(F32), ALU.mult,
                                               ALU.subtract).then_inc(hT_lo_ready, 1)
            dve.wait_ge(gate_act, 4)
            v.scalar_tensor_tensor(gate[0][:, :, :], gate[0][:, :, :], 0.0, gate[1][:, :, :], ALU.min,
                                   ALU.subtract).then_inc(gate_dve, 1)
            dve.wait_ge(xT_ready, 2 * C + B * C)
            v.memset(prod[:, 0:2], 0.0)
            v.memset(sq_sum[:, :], 0.0).then_inc(conv_step, 1)
            dve.wait_ge(conv_step, 1)
            with dve.Fori(0, CT) as i:
                for b in range(B):
                    dve.wait_ge(projected, 3 * B * i + (4 * B + b + 1))
                    base = 2 + b * BANK
                    v.tensor_tensor(prod[:, base:base + BANK], z_ps[b], at_block(gc_sb, b),
                                    ALU.mult).then_inc(evacuated, 1)
                    dve.wait_ge(evacuated, 2 * B * i + (B + b + 1))
                    v.tensor_scalar(at_block(gc_sb, b), prod[:, base:base + BANK],
                                    w_conv[:, 2, bass.ds(i, 1)], None, ALU.mult).then_inc(conv_step, 1)
                    for n, back in ((1, 1), (0, 2)):
                        dve.wait_ge(conv_step, 3 * B * i + (3 * b + back + 1))
                        v.scalar_tensor_tensor(at_block(gc_sb, b), prod[:, base - back:base - back + BANK],
                                               w_conv[:, n, bass.ds(i, 1)], at_block(gc_sb, b), ALU.mult,
                                               ALU.add).then_inc(conv_step, 1)
                for b in range(B):
                    dve.wait_ge(projected, 3 * B * i + (5 * B + b + 1))
                    dve.wait_ge(conv_step, 3 * B * i + (3 * b + 4))
                    dve.wait_ge(out_stored[b], DMA * i + DMA)
                    v.tensor_tensor(y_sb[:, b, :], z_ps[b], at_block(gc_sb, b), ALU.mult).then_inc(evacuated, 1)
                    dve.wait_ge(y_squared, B * i + (b + 1))
                    dve.wait_ge(sq_summed, B * i + (b + 1))
                    v.tensor_tensor(at_block(sq_sum, b), at_block(sq_sum, b), y_sq[:, :],
                                    ALU.add).then_inc(sq_summed, 1)
            dve.wait_ge(cum_ready, 1)
            v.tensor_copy(run[0][:, :, :].rearrange("p h t -> p (h t)"), psum[:, 3, 0:T * H]).then_inc(gate_dve, 1)
            for n, step in enumerate((1, 2, 4, 8)):
                src, dst = run[n % 2], run[(n + 1) % 2]
                dve.wait_ge(gate_dve, 2 * n + 2)
                v.tensor_tensor(dst[:, :, step:T], src[:, :, step:T], src[:, :, 0:T - step],
                                ALU.add).then_inc(gate_dve, 1)
                v.tensor_copy(dst[:, :, 0:step], src[:, :, 0:step]).then_inc(gate_dve, 1)
            dve.wait_ge(gate_dve, 10)
            v.tensor_copy(fcum[:, :, 0:1], logit_ps[:, :, 0:1])
            v.tensor_tensor(fcum[:, :, 1:T], logit_ps[:, :, 1:T], run[0][:, :, 0:T - 1],
                            ALU.add).then_inc(gate_dve, 1)
            dve.wait_ge(gate_act, 6)
            for n, hi in ((3, 2), (1, 0)):
                v.scalar_tensor_tensor(f_parts[:, n, :], fcum[:, :, :].rearrange("p h t -> p (h t)"),
                                       1.0 if hi == 2 else -1.0, f_parts[:, hi, :].bitcast(F32), ALU.mult,
                                       ALU.subtract).then_inc(gate_dve, 1)
            with dve.Fori(0, CT) as i:
                for t in range(3):
                    for b in range(B):
                        dve.wait_ge(projected, 3 * B * i + (3 * B + 3 * B * CT + B * t + b + 1))
                        dve.wait_ge(out_stored[b], 3 * DMA * i + DMA * (CT + t + 1))
                        v.tensor_scalar(y_sb[:, b, :], z_ps[b], z.hd ** -0.5 if t == 0 else 1.0, None,
                                        ALU.mult).then_inc(evacuated, 1)
            dve.wait_ge(rows_turned, 1)
            v.tensor_copy(rows[:, :, :].rearrange("p r t -> p (r t)"), xT_ps[0]).then_inc(rows_ready, 1)
            dve.wait_ge(conv_rms_ready, 1)
            v.reciprocal(k["rstd_conv"][:, :], conv_rms[:, :])


def attend(nc, z, k, d):
    T, B, hd = z.tiles, z.blocks, z.hd
    PAIRS = z.heads // 2
    HALF = 2 * BANK
    V_ROW = 5
    FOLDS = T // 2
    ROWS = 2 * T
    PREPS = 5
    mix_v = d["mix"]

    def halves(r):
        width = (r + 1) * P
        return [(c, min(c + HALF, width)) for c in range(0, width, HALF)]

    def quads(r):
        return [(kt, min(kt + 4, r + 1)) for kt in range(0, r + 1, 4)]

    HEAD_HALVES = sum(len(halves(r)) for r in range(T))
    HEAD_QUADS = sum(len(quads(r)) for r in range(T))
    HEAD_TURNS = HEAD_QUADS + B
    BODY_TURNS = 2 * HEAD_TURNS + B

    def half_no(R, h):
        return HEAD_HALVES * (R // T) + sum(len(halves(r)) for r in range(R % T)) + h

    def v_quad(R, last):
        q = R % T - V_ROW
        return q if 0 <= q < B and R < ROWS and not (last and R >= T) else None

    def turn_no(R, q, last):
        return (HEAD_QUADS * (R // T) + sum(len(quads(r)) for r in range(R % T)) + q
                + sum(v_quad(n, last) is not None for n in range(R + 1)))

    def v_turn_no(R):
        return turn_no(R, 0, False) - 1

    def turns(last):
        return 2 * HEAD_TURNS - (B if last else 0)

    with ExitStack() as ctx:
        m = Memory(nc, ctx)
        q_raw = m.sb("q_raw", [P, z.seq])
        k_raw = m.sb("k_raw", [P, z.seq])
        v_raw = m.sb("v_raw", [P, z.seq])
        q_a = m.sb("q_a", [P, 2, z.seq], F32R)
        k_a = m.sb("k_a", [P, 2, z.seq], F32R)
        q_b = m.sb("q_b", [P, 2, z.seq], F32R)
        k_b = m.sb("k_b", [P, 2, z.seq], F32R)
        vals = m.sb("vals", [P, 2, T, 2 * hd], F32R)
        p_sb = m.sb("p_sb", [P, 2, z.seq])
        pT_hi = m.sb("pT_hi", [P, 2, T, 2 * P], F32R)
        pT_lo = m.sb("pT_lo", [P, 2, T, 2 * P], F32R)
        oT_sb = m.sb("oT_sb", [P, 2, 2 * P])
        o_sb = m.sb("o_sb", [P, T, P])
        o_sq = m.sb("o_sq", [P, T // 2, hd])
        sq_sum = m.sb("o_sq_sum", [P, T, hd])
        mix_sb = m.sb("mix_sb", [P, 2, BANK])
        part_max = m.sb("part_max", [P, 2, 2])
        neg_max = m.sb("neg_max", [P, 2, 1])
        den = m.sb("den", [P, 2, T, 2])
        rden = m.sb("rden", [P, 2, T])
        attn_ssq = m.sb("attn_ssq", [P, T])
        attn_rms = m.sb("attn_rms", [P, T])

        psum = m.ps("psum_b", [P, 8, BANK])
        score_ps = [psum[:, 2 * n:2 * n + 2, :].rearrange("p b c -> p (b c)") for n in range(2)]
        turn_ps = [psum[:, 4 + n, :] for n in range(2)]
        oT_ps = psum[:, 6, 0:2 * P]
        o_ps = psum[:, 7, :].rearrange("p (t c) -> p t c", c=hd)

        kq_loaded = m.sem("kq_loaded")
        v_loaded = m.sem("v_loaded")
        rows_loaded = m.sem("rows_loaded")
        ones_set = m.sem("ones_set")
        prepped = m.sem("prepped")
        scored = m.sem("scored")
        max_part = m.sem("max_part")
        max_ready = m.sem("max_ready")
        exp_done = m.sem("exp_done")
        turned = m.sem("turned")
        hi_ready = m.sem("hi_ready")
        turn_free = m.sem("turn_free")
        summed = m.sem("summed")
        oT_out = m.sem("oT_out")
        folded = m.sem("folded")
        den_step = m.sem("den_step")
        o_out = m.sem("o_out")
        squared = m.sem("squared")
        mix_out = [m.sem(f"mix_out{n}") for n in range(2)]
        attn_step = m.sem("attn_step")

        block = ctx.enter_context(nc.Block())

        @block.sync
        def _(sp):
            def load(head, par, wait_turned, wait_scored):
                rows = bass.ds(hd * head, hd)
                for half in range(2):
                    at = slice(hd * half, hd * half + hd)
                    sp.dma_start(q_raw[at, :], d["qkv"][0, rows, :]).then_inc(kq_loaded, DMA)
                    sp.dma_start(k_raw[at, :], d["qkv"][1, rows, :]).then_inc(kq_loaded, DMA)
                if par == 0:
                    wait_turned()
                    sp.dma_start(v_raw[:, :], d["qkv"][2, bass.ds(hd * head, P), :]).then_inc(v_loaded, DMA)
                wait_scored()
                for rows_of, to, at in ((0, k_b, hd), (2, q_b, hd + 2)):
                    sp.dma_start(to[at:at + 2, par, :].bitcast(F32),
                                 d["gate_rows"][rows_of:rows_of + 2, bass.ds(head, 1), :]
                                 .rearrange("r h t -> (r h) t")).then_inc(rows_loaded, DMA)

            def body(i, last):
                for u in range(2):
                    if not (last and u == 1):
                        sp.wait_ge(prepped, 2 * PREPS * i + PREPS * (u + 1))
                        load(2 * i + (u + 1), 1 - u,
                             lambda: sp.wait_ge(turned, BODY_TURNS * i + (B + v_turn_no(V_ROW + B - 1) + 1)),
                             lambda: sp.wait_ge(scored, 2 * HEAD_HALVES * i + (HEAD_HALVES * u + 1)))
                for q in range(B):
                    sp.wait_ge(turn_free, BODY_TURNS * i + (2 + B + turns(last) + q + 1))
                    sp.dma_start(mix_v[bass.ds(P * i + z.conv, P), q * BANK:(q + 1) * BANK],
                                 mix_sb[:, q % 2, :]).then_inc(mix_out[q % 2], DMA)

            load(0, 0, lambda: None, lambda: sp.wait_ge(ones_set, 3))
            with sp.Fori(0, PAIRS - 1) as i:
                body(i, False)
            body(PAIRS - 1, True)
            for n in range(2):
                sp.wait_ge(mix_out[n], DMA * (1 + 2 * PAIRS))

        @block.gpsimd
        def _(pool):
            g = nc.gpsimd
            ones = [t[hd:hd + 4, :, :].bitcast(F32) for t in (q_b, k_b)]
            g.memset(den[:, :, :, :], 0.0).then_inc(ones_set, 1)
            g.memset(sq_sum[:, :, :], 0.0).then_inc(squared, 1)
            pool.wait_ge(squared, 1)
            g.memset(ones[0], 1.0).then_inc(ones_set, 1)
            g.memset(ones[1], 1.0).then_inc(ones_set, 1)
            pool.wait_ge(ones_set, 3)

            def prepare(n, par, first):
                def at(per, c):
                    return 2 * per * n[0] + (per * n[1] + c)
                top, low = slice(0, hd), slice(hd, 2 * hd)
                wide = k["zero"][:, :].broadcast_to([P, z.seq])
                pool.wait_ge(kq_loaded, at(4 * DMA, 4 * DMA))
                if not first:
                    pool.wait_ge(scored, at(HEAD_HALVES, 1 - HEAD_HALVES))
                g.tensor_tensor(q_a[:, par, :], q_raw[:, :], wide, ALU.add).then_inc(prepped, 1)
                g.tensor_tensor(q_b[top, par, :], q_raw[top, :], wide[top], ALU.add).then_inc(prepped, 1)
                g.tensor_tensor(k_a[:, par, :], k_raw[:, :], wide, ALU.add).then_inc(prepped, 1)
                pool.wait_ge(prepped, at(PREPS, 3))
                g.tensor_tensor(q_a[low, par, :], q_raw[low, :], q_a[low, par, :].bitcast(F32),
                                ALU.subtract).then_inc(prepped, 1)
                pool.wait_ge(prepped, at(PREPS, 4))
                g.tensor_tensor(k_b[top, par, :], k_raw[top, :], k_a[top, par, :].bitcast(F32),
                                ALU.subtract).then_inc(prepped, 1)

            def body(i, last):
                for u in range(2):
                    if last and u == 1:
                        break
                    prepare((i, u + 1), 1 - u, False)
                    squares(i, u)
                if last:
                    squares(i, 1)

            def squares(i, u):
                for half in range(2):
                    no = 2 * u + half
                    tiles = slice(half * T // 2, (half + 1) * T // 2)
                    pool.wait_ge(o_out, 4 * i + (no + 2))
                    pool.wait_ge(squared, 8 * i + (2 * no + 1))
                    o = o_sb[:, tiles, hd * u:hd * (u + 1)]
                    g.tensor_tensor(o_sq[:, :, :], o, o, ALU.mult).then_inc(squared, 1)
                    pool.wait_ge(squared, 8 * i + (2 * no + 2))
                    g.tensor_tensor(sq_sum[:, tiles, :], sq_sum[:, tiles, :], o_sq[:, :, :],
                                    ALU.add).then_inc(squared, 1)

            prepare((0, 0), 0, True)
            pool.wait_ge(scored, 1)
            with pool.Fori(0, PAIRS - 1) as i:
                body(i, False)
            body(PAIRS - 1, True)

        @block.tensor
        def _(pe):
            ident = k["ident"]

            def turn_v(q, no):
                for t in range(4):
                    last = nc.tensor.transpose(turn_ps[no % 2][:, t * P:(t + 1) * P],
                                               v_raw[:, (4 * q + t) * P:(4 * q + t + 1) * P], ident[:, :])
                last.then_inc(turned, 1)

            def score(i, R):
                u, r = R // T, R % T
                if r == 0:
                    pe.wait_ge(prepped, 2 * PREPS * i + PREPS * (u + 1))
                    pe.wait_ge(rows_loaded, 4 * DMA * i + 2 * DMA * (u + 1))
                for h, (lo, hi) in enumerate(halves(r)):
                    no = half_no(R, h)
                    region = score_ps[no % 2]
                    pe.wait_ge(exp_done, 2 * HEAD_HALVES * i + (no + 1))
                    for c in range(lo, hi, BANK):
                        e = min(c + BANK, hi)
                        to = region[:, c - lo:e - lo]
                        diagonal = e == (r + 1) * P
                        nc.tensor.matmul(to, q_a[:, u, r * P:(r + 1) * P], k_a[:, u, c:e], start=True, stop=False)
                        end = nc.tensor.matmul(to, q_b[0:hd + 4, u, r * P:(r + 1) * P], k_b[0:hd + 4, u, c:e],
                                               start=False, stop=not diagonal)
                        if diagonal:
                            end = nc.tensor.matmul(region[:, e - lo - P:e - lo], k["ident_bf"][:, :],
                                                   k["causal"][:, :], start=False, stop=True)
                    end.then_inc(scored, 1)

            def turn(i, R, last):
                r = R % T
                for q, (k0, k1) in enumerate(quads(r)):
                    no = turn_no(R, q, last)
                    pe.wait_ge(exp_done, 2 * HEAD_HALVES * i + (half_no(R, q // 2) + 3))
                    pe.wait_ge(turn_free, BODY_TURNS * i + (B + no + 1))
                    for kt in range(k0, k1):
                        end = nc.tensor.transpose(turn_ps[no % 2][:, (kt - k0) * P:(kt - k0 + 1) * P],
                                                  p_sb[:, R % 2, kt * P:(kt + 1) * P], ident[:, :])
                    end.then_inc(turned, 1)

            def sum_values(i, G, half, last):
                u, g = G // FOLDS, G % FOLDS
                if half == 0:
                    pe.wait_ge(turn_free, BODY_TURNS * i + (2 + B + turn_no(2 * G + 1, len(quads(2 * g + 1)), last)))
                    pe.wait_ge(oT_out, 2 * FOLDS * i + (G + 1))
                for kt in range(half * (g + 1), (half + 1) * (g + 1)):
                    q0 = P if kt == 2 * g + 1 else 0
                    for n, part in enumerate((pT_hi, pT_lo)):
                        end = nc.tensor.matmul(oT_ps[:, q0:2 * P], vals[:, u, kt, :], part[:, G % 2, kt, q0:2 * P],
                                               start=kt == 0 and n == 0, stop=kt == 2 * g + 1 and n == 1)
                if half == 1:
                    end.then_inc(summed, 1)

            def fold(i, G):
                g = G % FOLDS
                pe.wait_ge(oT_out, 2 * FOLDS * i + (G + 2))
                if g % (FOLDS // 2) == 0:
                    pe.wait_ge(o_out, 4 * i + (2 * (G // FOLDS) + g // (FOLDS // 2) + 1))
                for t in range(2):
                    end = nc.tensor.matmul(o_ps[:, (2 * g + t) % (T // 2), :], oT_sb[:, G % 2, t * P:(t + 1) * P],
                                           k["fold"][:, :], start=True, stop=True)
                end.then_inc(folded, 1)

            def body(i, last):
                for R in range(ROWS + 3):
                    if R < ROWS:
                        score(i, R)
                    if R >= 3 and R % 2 == 1 and (R - 3) // 2 < 2 * FOLDS:
                        sum_values(i, (R - 3) // 2, 1, last)
                    if R >= 4 and R % 2 == 0 and (R - 4) // 2 < 2 * FOLDS - 1:
                        fold(i, (R - 4) // 2)
                    if 1 <= R <= ROWS:
                        turn(i, R - 1, last)
                    if v_quad(R, last) is not None:
                        if v_quad(R, last) == 0:
                            pe.wait_ge(v_loaded, DMA * i + DMA * (R // T + 1))
                        pe.wait_ge(turn_free, BODY_TURNS * i + (B + v_turn_no(R) + 1))
                        turn_v(v_quad(R, last), v_turn_no(R))
                    if R >= 2 and R % 2 == 0 and (R - 2) // 2 < 2 * FOLDS:
                        sum_values(i, (R - 2) // 2, 0, last)
                fold(i, 2 * FOLDS - 1)
                pe.wait_ge(o_out, 4 * i + 5)
                for q in range(B):
                    no = turns(last) + q
                    pe.wait_ge(turn_free, BODY_TURNS * i + (B + no + 1))
                    for t in range(4):
                        end = nc.tensor.transpose(turn_ps[no % 2][:, t * P:(t + 1) * P], o_sb[:, 4 * q + t, :],
                                                 ident[:, :])
                    end.then_inc(turned, 1)

            pe.sem_inc(summed, 2)
            pe.wait_ge(v_loaded, DMA)
            for q in range(B):
                pe.wait_ge(turn_free, q + 1)
                turn_v(q, q)
            with pe.Fori(0, PAIRS - 1) as i:
                body(i, False)
            body(PAIRS - 1, True)

        def quad_targets(tile, R, q):
            k0, k1 = quads(R % T)[q]
            return tile[:, (R // 2) % 2, k0:k1, (R % 2) * P:(R % 2 + 1) * P]

        def quad_ps(no, n, width):
            return turn_ps[no % 2][:, 0:n * width].rearrange("p (t c) -> p t c", c=width)

        @block.scalar
        def _(act):
            act.sem_inc(exp_done, 2)
            act.sem_inc(oT_out, 1)

            def v_high(par, q, no):
                nc.scalar.activation(vals[:, par, 4 * q:4 * q + 4, 0:hd], quad_ps(no, 4, P)[:, :, hd * par:hd * par + hd],
                                     ACT.Copy).then_inc(hi_ready, 1)

            def body(i, last):
                for R in range(ROWS + 3):
                    if R < ROWS:
                        act.wait_ge(max_ready, ROWS * i + (R + 1))
                        for h, (lo, hi) in enumerate(halves(R % T)):
                            region = score_ps[half_no(R, h) % 2]
                            nc.scalar.activation(p_sb[:, R % 2, lo:hi], region[:, 0:hi - lo], ACT.Exp,
                                                 bias=neg_max[:, R % 2, :],
                                                 accum_out=den[:, R // T, R % T, h:h + 1]).then_inc(exp_done, 1)
                    if R >= 3 and R % 2 == 1 and (R - 3) // 2 < 2 * FOLDS:
                        G = (R - 3) // 2
                        act.wait_ge(summed, 2 * FOLDS * i + (G + 3))
                        if G >= 2:
                            act.wait_ge(folded, 2 * FOLDS * i + (G - 1))
                        nc.scalar.activation(oT_sb[:, G % 2, :], oT_ps, ACT.Copy).then_inc(oT_out, 1)
                    if 1 <= R <= ROWS:
                        row = R - 1
                        act.wait_ge(summed, 2 * FOLDS * i + (row // 2 + 1))
                        for q, (k0, k1) in enumerate(quads(row % T)):
                            no = turn_no(row, q, last)
                            act.wait_ge(turned, BODY_TURNS * i + (B + no + 1))
                            nc.scalar.activation(quad_targets(pT_hi, row, q), quad_ps(no, k1 - k0, P),
                                                 ACT.Copy).then_inc(hi_ready, 1)
                    if v_quad(R, last) is not None:
                        act.wait_ge(turned, BODY_TURNS * i + (B + v_turn_no(R) + 1))
                        v_high(1 - R // T, v_quad(R, last), v_turn_no(R))

            act.wait_ge(ones_set, 1)
            for q in range(B):
                act.wait_ge(turned, q + 1)
                v_high(0, q, q)
            with act.Fori(0, PAIRS - 1) as i:
                body(i, False)
            body(PAIRS - 1, True)
            act.wait_ge(attn_step, 1)
            nc.scalar.activation(attn_rms[:, :], attn_ssq[:, :], ACT.Sqrt, bias=k["eps"][:, :],
                                 scale=1.0 / z.attn).then_inc(attn_step, 1)

        @block.vector
        def _(dve):
            v = nc.vector
            dve.sem_inc(turn_free, 2)
            dve.sem_inc(o_out, 1)
            PARTS = 2 * sum(len(halves(r)) == 2 for r in range(T)) * 2

            def v_low(par, q, no):
                v.tensor_tensor(vals[:, par, 4 * q:4 * q + 4, hd:2 * hd], quad_ps(no, 4, P)[:, :, hd * par:hd * par + hd],
                                vals[:, par, 4 * q:4 * q + 4, 0:hd].bitcast(F32), ALU.subtract).then_inc(turn_free, 1)

            def outputs(i, u, half):
                rows = slice(half * T // 2, (half + 1) * T // 2)
                step = 8 * i + (4 * u + 2 * half)
                dve.wait_ge(exp_done, 2 * HEAD_HALVES * i + (half_no(T * u + (half + 1) * T // 2 - 1, 0) +
                                                             len(halves((half + 1) * T // 2 - 1)) + 2))
                v.tensor_reduce(rden[:, u, rows], den[:, u, rows, :], AX.X, ALU.add).then_inc(den_step, 1)
                dve.wait_ge(den_step, step + 1)
                v.reciprocal(rden[:, u, rows], rden[:, u, rows]).then_inc(den_step, 1)
                dve.wait_ge(den_step, step + 2)
                dve.wait_ge(folded, 2 * FOLDS * i + (FOLDS * u + FOLDS // 2 * (half + 1)))
                if u == 0 and half == 0:
                    dve.wait_ge(squared, 8 * i + 1)
                    dve.wait_ge(turned, BODY_TURNS * i + B)
                v.tensor_tensor(o_sb[:, rows, hd * u:hd * (u + 1)], o_ps,
                                rden[:, u, rows].unsqueeze(2).broadcast_to([P, T // 2, hd]),
                                ALU.mult).then_inc(o_out, 1)

            def body(i, last):
                part = 0
                for R in range(ROWS + 3):
                    if R < ROWS:
                        r = R % T
                        n = len(halves(r))
                        for h, (lo, hi) in enumerate(halves(r)):
                            no = half_no(R, h)
                            dve.wait_ge(scored, 2 * HEAD_HALVES * i + (no + 1))
                            src = score_ps[no % 2][:, 0:hi - lo]
                            if n == 1:
                                v.tensor_reduce(neg_max[:, R % 2, :], src, AX.X, ALU.max,
                                                negate=True).then_inc(max_ready, 1)
                            else:
                                v.tensor_reduce(part_max[:, R % 2, h:h + 1], src, AX.X, ALU.max).then_inc(max_part, 1)
                                part += 1
                        if n == 2:
                            dve.wait_ge(max_part, PARTS * i + part)
                            v.tensor_reduce(neg_max[:, R % 2, :], part_max[:, R % 2, :], AX.X, ALU.max,
                                            negate=True).then_inc(max_ready, 1)
                    for G in (FOLDS // 2 - 1, FOLDS - 1, 3 * FOLDS // 2 - 1):
                        if R == 2 * G + 5:
                            outputs(i, G // FOLDS, G // (FOLDS // 2) % 2)
                    if 1 <= R <= ROWS:
                        row = R - 1
                        for q, (k0, k1) in enumerate(quads(row % T)):
                            no = turn_no(row, q, last)
                            dve.wait_ge(hi_ready, 2 * HEAD_TURNS * i + (B + no + 1))
                            v.tensor_tensor(quad_targets(pT_lo, row, q), quad_ps(no, k1 - k0, P),
                                            quad_targets(pT_hi, row, q).bitcast(F32),
                                            ALU.subtract).then_inc(turn_free, 1)
                    if v_quad(R, last) is not None:
                        dve.wait_ge(hi_ready, 2 * HEAD_TURNS * i + (B + v_turn_no(R) + 1))
                        v_low(1 - R // T, v_quad(R, last), v_turn_no(R))
                outputs(i, 1, 1)
                for q in range(B):
                    no = turns(last) + q
                    dve.wait_ge(turned, BODY_TURNS * i + (B + no + 1))
                    dve.wait_ge(mix_out[q % 2], 2 * DMA * i + DMA * (q // 2 + 1))
                    v.tensor_copy(mix_sb[:, q % 2, :], turn_ps[no % 2]).then_inc(turn_free, 1)

            for n in range(2):
                dve.sem_inc(mix_out[n], DMA)
            for q in range(B):
                dve.wait_ge(hi_ready, q + 1)
                v_low(0, q, q)
            with dve.Fori(0, PAIRS - 1) as i:
                body(i, False)
            body(PAIRS - 1, True)
            dve.wait_ge(squared, 1 + 8 * PAIRS)
            v.tensor_reduce(attn_ssq[:, :], sq_sum[:, :, :], AX.X, ALU.add).then_inc(attn_step, 1)
            dve.wait_ge(attn_step, 2)
            v.reciprocal(k["rstd_attn"][:, :], attn_rms[:, :])


def project_mix(nc, z, k, a, d):
    C, T = z.dc, z.tiles
    GC = z.conv // P
    HC = C // 2
    x_v, mix_v = a["x"][0], d["mix"].rearrange("(c p) t -> p c t", p=P)
    h_v = d["h2T"].rearrange("(c p) t -> p c t", p=P)

    with ExitStack() as ctx:
        m = Memory(nc, ctx)
        wo_raw = m.sb("wo_raw", [P, 2, z.d])
        wo_hi = m.sb("wo_hi", [P, C, z.d], F32R)
        wo_lo = m.sb("wo_lo", [P, C, z.d], F32R)
        g_out = m.sb("g_out", [P, C])
        g_ffn = m.sb("g_ffn_sb", [P, C])
        mix_raw = m.sb("mix_raw", [P, 2, C, P])
        mx_hi = m.sb("mx_hi", [P, 2, C, P], F32R)
        mx_lo = m.sb("mx_lo", [P, 2, C, P], F32R)
        x_sb = m.sb("x_sb", [P, 2, z.d])
        x1_sb = m.sb("x1_sb", [P, 2, z.d])
        xn_sb = m.sb("xn_sb", [P, 2, z.d])
        h_sb = m.sb("h_sb", [P, 2, C, P])
        junk = m.sb("junk_c", [P, z.d], BF16)
        ssq = m.sb("ssq_c", [P, 2])
        rms = m.sb("rms_c", [P, 2])
        rstd = m.sb("rstd_c", [P, 2])

        psum = m.ps("psum_c", [P, 8, BANK])
        turn_ps = [psum[:, 4 + n, :].rearrange("p (c t) -> p c t", t=P) for n in range(2)]

        vectors_loaded = m.sem("gains_loaded")
        wo_loaded = [m.sem(f"wo_loaded{n}") for n in range(2)]
        wo_hi_ready = m.sem("wo_hi_ready")
        wo_split = m.sem("wo_split")
        mix_loaded = [m.sem(f"mix_loaded{n}") for n in range(2)]
        x_loaded = [m.sem(f"xc_loaded{n}") for n in range(2)]
        mix_hi_ready = m.sem("mix_hi_ready")
        mix_split = m.sem("mix_split")
        mixed = m.sem("mixed")
        c_added = m.sem("c_added")
        x1_added = m.sem("x1_added")
        squared = m.sem("x1_squared")
        rms_ready = m.sem("rms_c_ready")
        rstd_ready = m.sem("rstd_c_ready")
        x_normed = m.sem("x1_normed")
        turned = m.sem("x1_turned")
        h_ready = m.sem("h_ready")
        x1_stored = [m.sem(f"x1_stored{n}") for n in range(2)]
        h_stored = [m.sem(f"h_stored{n}") for n in range(2)]

        ctx.enter_context(nc.allow_non_contiguous_dma(reason="small vectors, a channel per partition"))
        block = ctx.enter_context(nc.Block())

        def tiles(n):
            return bass.ds(2 * P * n[0] + P * n[1], P)

        def count(n, per, c):
            return 2 * per * n[0] + (per * n[1] + c)

        def run_steps(engine, step):
            step((0, 0), 0, True, False)
            with engine.Fori(0, T // 2 - 1) as i:
                step((i, 1), 1, False, False)
                step((i, 2), 0, False, False)
            step((0, T - 1), 1, False, True)

        @block.sync
        def _(sp):
            for n, name in enumerate(("g_conv_out", "g_attn_out")):
                sp.dma_start(g_out[:, GC * n:GC * (n + 1)], a[name][0].rearrange("(c p) -> p c", p=P)) \
                    .then_inc(vectors_loaded, DMA)
            sp.dma_start(g_ffn[:, :], a["g_ffn"][0].rearrange("(c p) -> p c", p=P)).then_inc(vectors_loaded, DMA)

            def load(n, u):
                sp.wait_ge(mix_split, count(n, 1, 1))
                sp.dma_start(mix_raw[:, u, :, :], mix_v[:, :, tiles(n)]).then_inc(mix_loaded[u], DMA)
                sp.wait_ge(x1_added, count(n, 2, 2))
                sp.dma_start(x_sb[:, u, :], x_v[tiles(n), :]).then_inc(x_loaded[u], DMA)

            for c in range(C):
                if c >= 2:
                    sp.wait_ge(wo_split, c - 1)
                sp.dma_start(wo_raw[:, c % 2, :], a["w_o"][0][c * P:(c + 1) * P, :]).then_inc(wo_loaded[c % 2], DMA)
            with sp.Fori(0, T // 2) as i:
                for u in range(2):
                    load((i, u), u)
            for u in range(2):
                sp.wait_ge(x1_stored[u], DMA * (1 + T // 2))
                sp.wait_ge(h_stored[u], DMA * (1 + T // 2))

        @block.scalar
        def _(act):
            act.wait_ge(vectors_loaded, 3 * DMA)
            act.sem_inc(squared, 1)
            for u in range(2):
                act.sem_inc(x1_stored[u], DMA)
                act.sem_inc(h_stored[u], DMA)
            for c in range(C):
                act.wait_ge(wo_loaded[c % 2], DMA * (c // 2 + 1))
                nc.scalar.activation(wo_hi[:, c, :], wo_raw[:, c % 2, :], ACT.Copy,
                                     scale=g_out[:, c:c + 1]).then_inc(wo_hi_ready, 1)

            def mix_high(n, u, slot_is_new):
                act.wait_ge(mix_loaded[u], count(n, DMA // 2, DMA - DMA // 2 * u))
                if not slot_is_new:
                    act.wait_ge(mixed, count(n, 2, -2))
                nc.scalar.activation(mx_hi[:, u, :, :], mix_raw[:, u, :, :], ACT.Copy).then_inc(mix_hi_ready, 1)

            def step(n, u, first, last):
                if first:
                    mix_high((0, 0), 0, True)
                if not last:
                    mix_high((n[0], n[1] + 1), 1 - u, first)
                act.wait_ge(x1_added, count(n, 2, 6))
                act.wait_ge(squared, count(n, 1, 1))
                nc.scalar.activation(junk[:, :], x1_sb[:, u, :], ACT.Square,
                                     accum_out=ssq[:, u:u + 1]).then_inc(squared, 1)
                act.dma_start(d["x1"][tiles(n), :], x1_sb[:, u, :]).then_inc(x1_stored[u], DMA)
                act.wait_ge(squared, count(n, 1, 2))
                nc.scalar.activation(rms[:, u:u + 1], ssq[:, u:u + 1], ACT.Sqrt, bias=k["eps"][:, :],
                                     scale=1.0 / z.d).then_inc(rms_ready, 1)
                if not first:
                    store_h((n[0], n[1] - 1), 1 - u)
                if last:
                    store_h(n, u)

            def store_h(n, u):
                act.wait_ge(h_ready, count(n, 2, 4))
                act.dma_start(h_v[:, :, tiles(n)], h_sb[:, u, :, :]).then_inc(h_stored[u], DMA)

            run_steps(act, step)

        @block.vector
        def _(dve):
            v = nc.vector
            dve.sem_inc(mix_split, 2)
            dve.sem_inc(x1_added, 4)
            dve.sem_inc(h_ready, 2)
            for c in range(C):
                dve.wait_ge(wo_hi_ready, c + 1)
                v.scalar_tensor_tensor(wo_lo[:, c, :], wo_raw[:, c % 2, :], g_out[:, c:c + 1],
                                       wo_hi[:, c, :].bitcast(F32), ALU.mult, ALU.subtract).then_inc(wo_split, 1)

            def mix_low(n, u):
                dve.wait_ge(mix_hi_ready, count(n, 1, 1))
                v.tensor_tensor(mx_lo[:, u, :, :], mix_raw[:, u, :, :], mx_hi[:, u, :, :].bitcast(F32),
                                ALU.subtract).then_inc(mix_split, 1)

            def high_half(n, u):
                dve.wait_ge(h_stored[u], count(n, DMA // 2, DMA - DMA // 2 * u))
                for h in range(2):
                    dve.wait_ge(turned, count(n, 2, h + 1))
                    v.tensor_tensor(h_sb[:, u, HC * h:HC * (h + 1), :], turn_ps[h],
                                    g_ffn[:, HC * h:HC * (h + 1)].unsqueeze(2).broadcast_to([P, HC, P]),
                                    ALU.mult).then_inc(h_ready, 1)

            def step(n, u, first, last):
                if first:
                    mix_low((0, 0), 0)
                if not last:
                    mix_low((n[0], n[1] + 1), 1 - u)
                dve.wait_ge(x_loaded[u], count(n, DMA // 2, DMA - DMA // 2 * u))
                dve.wait_ge(x1_stored[u], count(n, DMA // 2, DMA - DMA // 2 * u))
                for h in range(2):
                    cols = slice(h * BANK, (h + 1) * BANK)
                    dve.wait_ge(mixed, count(n, 2, h + 1))
                    v.scalar_tensor_tensor(x1_sb[:, u, cols], psum[:, 2 * h, :],
                                           k["rstd_conv"][:, bass.ds(2 * n[0] + n[1], 1)], x_sb[:, u, cols],
                                           ALU.mult, ALU.add).then_inc(c_added, 1)
                    dve.wait_ge(c_added, count(n, 2, h + 1))
                    v.scalar_tensor_tensor(x1_sb[:, u, cols], psum[:, 2 * h + 1, :],
                                           k["rstd_attn"][:, bass.ds(2 * n[0] + n[1], 1)], x1_sb[:, u, cols],
                                           ALU.mult, ALU.add).then_inc(x1_added, 1)
                if not first:
                    high_half((n[0], n[1] - 1), 1 - u)
                dve.wait_ge(rms_ready, count(n, 1, 1))
                v.reciprocal(rstd[:, u:u + 1], rms[:, u:u + 1]).then_inc(rstd_ready, 1)
                dve.wait_ge(rstd_ready, count(n, 1, 1))
                v.tensor_scalar(xn_sb[:, u, :], x1_sb[:, u, :], rstd[:, u:u + 1], None,
                                ALU.mult).then_inc(x_normed, 1)
                if last:
                    high_half(n, u)

            run_steps(dve, step)

        @block.tensor
        def _(pe):
            pe.wait_ge(wo_split, C)

            def turn(n, u):
                pe.wait_ge(x_normed, count(n, 1, 1))
                for h in range(2):
                    pe.wait_ge(h_ready, count(n, 2, h + 1))
                    for c in range(HC):
                        end = nc.tensor.transpose(turn_ps[h][:, c, :],
                                                  xn_sb[:, u, (HC * h + c) * P:(HC * h + c + 1) * P], k["ident"][:, :])
                    end.then_inc(turned, 1)

            def step(n, u, first, last):
                pe.wait_ge(mix_split, count(n, 1, 3))
                for h in range(2):
                    pe.wait_ge(x1_added, count(n, 2, h + 3))
                    cols = slice(h * BANK, (h + 1) * BANK)
                    for group in range(2):
                        end = split_product(nc, psum[:, 2 * h + group, :],
                                            [(mx_hi[:, u, c, :], mx_lo[:, u, c, :], wo_hi[:, c, cols], wo_lo[:, c, cols])
                                             for c in range(GC * group, GC * (group + 1))], True, True)
                    end.then_inc(mixed, 1)
                if not first:
                    turn((n[0], n[1] - 1), 1 - u)
                if last:
                    turn(n, u)

            run_steps(pe, step)


def feed_forward(nc, z, k, a, d, out):
    C, F = z.dc, z.ff // P
    HT = z.seq // 2
    TT, HB = HT // P, HT // BANK
    UPS = 2 * HB
    DOWNS = TT * (z.d // BANK)
    STEPS = 5
    up_v = a["w_up"][0].rearrange("(c p) n -> p c n", p=P)
    down_v = a["w_down"][0]
    h_v = d["h2T"].rearrange("(c p) t -> c p t", p=P)
    x1_v = d["x1"].rearrange("(f t p) c -> f p t c", p=P, t=TT)
    out_v = out[0].rearrange("(f t p) c -> f t p c", p=P, t=TT)

    with ExitStack() as ctx:
        m = Memory(nc, ctx)
        h_raw = m.sb("h_raw", [P, 2, HT])
        h_hi = m.sb("h_hi", [P, C, HT], F32R)
        h_lo = m.sb("h_lo", [P, C, HT], F32R)
        acc = m.sb("acc", [P, TT, z.d])
        up_raw = m.sb("up_raw", [P, 2, C, P])
        up_hi = m.sb("up_hi", [P, 2, 2, C, P], F32R)
        up_lo = m.sb("up_lo", [P, 2, 2, C, P], F32R)
        down_raw = m.sb("down_raw", [P, z.d])
        down_hi = m.sb("down_hi", [P, 2, z.d], F32R)
        down_lo = m.sb("down_lo", [P, 2, z.d], F32R)
        z_sb = m.sb("z_sb", [P, 2, 2 + HT])
        u_sb = m.sb("u_sb", [P, 2, HT])
        act_hi = m.sb("act_hi", [P, 2, HT], F32R)
        act_lo = m.sb("act_lo", [P, 2, HT], F32R)
        carry = m.sb("carry", [P, 2, F, 2])
        g_final = m.sb("g_final_sb", [P, z.d])
        junk = m.sb("junk_d", [P, z.d], BF16)
        ssq = m.sb("ssq_d", [P, TT])
        rms = m.sb("rms_d", [P, TT])
        rstd = m.sb("rstd_d", [P, TT])
        w_conv = k["w_ffn_conv"]

        psum = m.ps("psum_d", [P, 8, BANK])
        up_ps = [psum[:, n, :] for n in range(UPS)]
        down_ps = [psum[:, 4 + n, :] for n in range(4)]

        g_loaded = m.sem("g_final_loaded")
        h_loaded = [m.sem(f"h_loaded{n}") for n in range(2)]
        h_hi_ready = m.sem("h_hi_ready")
        h_split = m.sem("h_split")
        up_loaded = [m.sem(f"up_loaded{n}") for n in range(2)]
        up_hi_ready = m.sem("up_hi_ready")
        up_split = m.sem("up_split")
        down_loaded = m.sem("down_loaded")
        down_hi_ready = m.sem("down_hi_ready")
        down_split = m.sem("down_split")
        acc_loaded = m.sem("acc_loaded")
        up_done = m.sem("up_done")
        z_out = m.sem("z_out")
        padded = m.sem("padded")
        conv_step = m.sem("ffn_step")
        gated = m.sem("gated")
        act_hi_ready = m.sem("act_hi_ready")
        act_ready = m.sem("act_ready")
        down_done = m.sem("down_done")
        acc_added = m.sem("acc_added")
        squared = m.sem("acc_squared")
        rms_ready = m.sem("rms_d_ready")
        rstd_ready = m.sem("rstd_d_ready")
        out_ready = m.sem("out_ready")
        out_stored = m.sem("out_stored")

        block = ctx.enter_context(nc.Block())

        def count(f, n, per, c):
            return per * F * f + (2 * per * n[0] + (per * n[1] + c))

        @block.sync
        def _(sp):
            sp.dma_start(g_final[:, :], a["g_final"].partition_broadcast(P)).then_inc(g_loaded, DMA)
            with sp.Fori(0, 2) as f:
                for c in range(C):
                    sp.wait_ge(h_split, C * f + (c + 1))
                    sp.dma_start(h_raw[:, c % 2, :], h_v[c, :, bass.ds(HT * f, HT)]).then_inc(h_loaded[c % 2], DMA)
                with sp.Fori(1, F // 2 + 1) as i:
                    for u in range(2):
                        n = (i, u - 2)
                        for t in range(2):
                            sp.wait_ge(up_split, count(f, n, 2, t + 1))
                            sp.dma_start(up_raw[:, t, :, :],
                                         up_v[:, :, bass.ds(2 * P * i + (P * (u - 2) + z.ff * t), P)]) \
                                .then_inc(up_loaded[t], DMA)
                        sp.wait_ge(down_split, count(f, n, 1, 1))
                        sp.dma_start(down_raw[:, :], down_v[bass.ds(2 * P * i + P * (u - 2), P), :]) \
                            .then_inc(down_loaded, DMA)
            sp.wait_ge(out_stored, DMA * (1 + 2 * TT))

        @block.gpsimd
        def _(pool):
            g = nc.gpsimd
            pool.sem_inc(up_split, 2)
            pool.sem_inc(down_split, 1)
            zero = k["zero"][:, :]
            wide_up, wide_down = zero.unsqueeze(2).broadcast_to([P, C, P]), zero.broadcast_to([P, z.d])
            with pool.Fori(0, 2) as f:
                with pool.Fori(0, F // 2) as i:
                    for u in range(2):
                        n = (i, u)
                        for t in range(2):
                            pool.wait_ge(up_loaded[t], count(f, n, DMA, DMA))
                            if t == 0:
                                pool.wait_ge(up_done, count(f, n, UPS, UPS))
                            g.tensor_tensor(up_hi[:, u, t, :, :], up_raw[:, t, :, :], wide_up,
                                            ALU.add).then_inc(up_hi_ready, 1)
                            pool.wait_ge(up_hi_ready, count(f, n, 2, t + 1))
                            g.tensor_tensor(up_lo[:, u, t, :, :], up_raw[:, t, :, :],
                                            up_hi[:, u, t, :, :].bitcast(F32), ALU.subtract).then_inc(up_split, 1)
                        pool.wait_ge(down_loaded, count(f, n, DMA, DMA))
                        pool.wait_ge(down_done, count(f, n, DOWNS, DOWNS))
                        g.tensor_tensor(down_hi[:, u, :], down_raw[:, :], wide_down, ALU.add).then_inc(down_hi_ready, 1)
                        pool.wait_ge(down_hi_ready, count(f, n, 1, 1))
                        g.tensor_tensor(down_lo[:, u, :], down_raw[:, :], down_hi[:, u, :].bitcast(F32),
                                        ALU.subtract).then_inc(down_split, 1)

        def run_steps(engine, f, step):
            step(f, (0, 0), 0, True, False)
            with engine.Fori(0, F // 2 - 1) as i:
                step(f, (i, 1), 1, False, False)
                step(f, (i, 2), 0, False, False)
            step(f, (0, F - 1), 1, False, True)

        @block.tensor
        def _(pe):
            pe.sem_inc(up_done, 2 * UPS)
            pe.sem_inc(down_done, 2 * DOWNS)

            def up(f, n, u):
                for t in range(2):
                    pe.wait_ge(up_split, count(f, n, 2, t + 3))
                    for b in range(HB):
                        bank = HB * t + b
                        cols = slice(b * BANK, (b + 1) * BANK)
                        pe.wait_ge(z_out, count(f, n, UPS, bank + 1))
                        split_product(nc, up_ps[bank],
                                      [(up_hi[:, u, t, c, :], up_lo[:, u, t, c, :], h_hi[:, c, cols], h_lo[:, c, cols])
                                       for c in range(C)], True, True).then_inc(up_done, 1)

            def down(f, n, u):
                pe.wait_ge(act_ready, count(f, n, 1, 2))
                pe.wait_ge(down_split, count(f, n, 1, 2))
                for t in range(TT):
                    rows = slice(t * P, (t + 1) * P)
                    for h in range(2):
                        no = 2 * t + h
                        cols = slice(h * BANK, (h + 1) * BANK)
                        pe.wait_ge(acc_added, count(f, n, DOWNS, no + 1))
                        split_product(nc, down_ps[no % 4],
                                      [(act_hi[:, u, rows], act_lo[:, u, rows], down_hi[:, u, cols],
                                        down_lo[:, u, cols])], True, True).then_inc(down_done, 1)

            def step(f, n, u, first, last):
                up(f, n, u)
                if not first:
                    down(f, (n[0], n[1] - 1), 1 - u)
                if last:
                    down(f, n, u)

            with pe.Fori(0, 2) as f:
                pe.wait_ge(h_split, C * f + (C + 2))
                run_steps(pe, f, step)

        @block.scalar
        def _(act):
            act.sem_inc(z_out, UPS)
            act.sem_inc(squared, 1)
            act.sem_inc(out_stored, DMA)
            with act.Fori(0, 2) as f:
                act.wait_ge(up_done, UPS * F * f + 2 * UPS)
                for c in range(C):
                    act.wait_ge(h_loaded[c % 2], DMA * (C // 2) * f + DMA * (c // 2 + 1))
                    nc.scalar.activation(h_hi[:, c, :], h_raw[:, c % 2, :], ACT.Copy).then_inc(h_hi_ready, 1)
                act.wait_ge(out_stored, DMA * TT * f + DMA)
                act.dma_start(acc[:, :, :], x1_v[bass.ds(f, 1), :, :, :].rearrange("o p t c -> (o p) t c")) \
                    .then_inc(acc_loaded, DMA)
                with act.Fori(0, F // 2) as i:
                    for u in range(2):
                        n = (i, u)
                        act.wait_ge(act_ready, count(f, n, 1, 1))
                        for t in range(2):
                            for b in range(HB):
                                bank = HB * t + b
                                at = b * BANK
                                act.wait_ge(up_done, count(f, n, UPS, 2 * UPS + bank + 1))
                                nc.scalar.activation(z_sb[:, t, 2 + at:2 + at + BANK], up_ps[bank], ACT.Copy)
                                nc.scalar.activation(u_sb[:, t, at:at + BANK], up_ps[bank], ACT.Copy,
                                                     scale=w_conv[:, z.taps - 1, bass.ds(2 * i + (u + F * t), 1)]) \
                                    .then_inc(z_out, 1)
                        act.wait_ge(conv_step, count(f, n, STEPS, 4))
                        nc.scalar.activation(u_sb[:, 1, :], u_sb[:, 1, :], ACT.Silu).then_inc(gated, 1)
                        act.wait_ge(conv_step, count(f, n, STEPS, 5))
                        act.wait_ge(down_done, count(f, n, DOWNS, DOWNS))
                        nc.scalar.activation(act_hi[:, u, :], u_sb[:, 0, :], ACT.Copy).then_inc(act_hi_ready, 1)
                for t in range(TT):
                    act.wait_ge(acc_added, count(f, (0, F - 1), DOWNS, 4 + 2 * (t + 1)))
                    act.wait_ge(squared, TT * f + (t + 1))
                    nc.scalar.activation(junk[:, :], acc[:, t, :], ACT.Square,
                                         accum_out=ssq[:, t:t + 1]).then_inc(squared, 1)
                    act.wait_ge(squared, TT * f + (t + 2))
                    nc.scalar.activation(rms[:, t:t + 1], ssq[:, t:t + 1], ACT.Sqrt, bias=k["eps"][:, :],
                                         scale=1.0 / z.d).then_inc(rms_ready, 1)
                for t in range(TT):
                    act.wait_ge(out_ready, TT * f + (t + 1))
                    act.dma_start(out_v[bass.ds(f, 1), t, :, :].rearrange("o p c -> (o p) c"), acc[:, t, :]) \
                        .then_inc(out_stored, DMA)

        @block.vector
        def _(dve):
            v = nc.vector
            dve.sem_inc(h_split, 2)
            dve.sem_inc(act_ready, 1)
            dve.sem_inc(acc_added, 4)
            v.memset(carry[:, :, :, :], 0.0).then_inc(padded, 1)
            dve.wait_ge(padded, 1)

            def add_share(f, n):
                for no in range(DOWNS):
                    at = (slice(None), no // 2, slice(no % 2 * BANK, (no % 2 + 1) * BANK))
                    dve.wait_ge(down_done, count(f, n, DOWNS, 2 * DOWNS + no + 1))
                    v.tensor_tensor(acc[at], down_ps[no % 4], acc[at], ALU.add).then_inc(acc_added, 1)

            def step(f, n, u, first, last):
                if first:
                    dve.wait_ge(acc_loaded, DMA * f + DMA)
                else:
                    add_share(f, (n[0], n[1] - 1))
                tile = bass.ds(2 * n[0] + n[1], 1)
                dve.wait_ge(z_out, count(f, n, UPS, 2 * UPS))
                v.tensor_scalar(z_sb[:, :, 0:2], carry[:, :, tile, :].rearrange("p a o b -> p a (o b)"), 1.0,
                                None, ALU.mult) \
                    .then_inc(padded, 1)
                dve.wait_ge(padded, count(f, n, 2, 2))
                v.tensor_scalar(carry[:, :, tile, :].rearrange("p a o b -> p a (o b)"), z_sb[:, :, HT:HT + 2], 1.0,
                                None, ALU.mult) \
                    .then_inc(padded, 1)
                for back in (1, 2):
                    for t in range(2):
                        if back == 2:
                            dve.wait_ge(conv_step, count(f, n, STEPS, t + 1))
                        v.scalar_tensor_tensor(u_sb[:, t, :], z_sb[:, t, 2 - back:2 - back + HT],
                                               w_conv[:, z.taps - 1 - back, bass.ds(2 * n[0] + (n[1] + F * t), 1)],
                                               u_sb[:, t, :], ALU.mult, ALU.add).then_inc(conv_step, 1)
                dve.wait_ge(gated, count(f, n, 1, 1))
                v.tensor_tensor(u_sb[:, 0, :], u_sb[:, 0, :], u_sb[:, 1, :], ALU.mult).then_inc(conv_step, 1)
                dve.wait_ge(act_hi_ready, count(f, n, 1, 1))
                v.tensor_tensor(act_lo[:, u, :], u_sb[:, 0, :], act_hi[:, u, :].bitcast(F32),
                                ALU.subtract).then_inc(act_ready, 1)
                if last:
                    add_share(f, n)

            with dve.Fori(0, 2) as f:
                for c in range(C):
                    dve.wait_ge(h_hi_ready, C * f + (c + 1))
                    v.tensor_tensor(h_lo[:, c, :], h_raw[:, c % 2, :], h_hi[:, c, :].bitcast(F32),
                                    ALU.subtract).then_inc(h_split, 1)
                run_steps(dve, f, step)
                dve.wait_ge(g_loaded, DMA)
                for t in range(TT):
                    dve.wait_ge(rms_ready, TT * f + (t + 1))
                    v.reciprocal(rstd[:, t:t + 1], rms[:, t:t + 1]).then_inc(rstd_ready, 1)
                    dve.wait_ge(rstd_ready, TT * f + (t + 1))
                    v.scalar_tensor_tensor(acc[:, t, :], acc[:, t, :], rstd[:, t:t + 1], g_final[:, :], ALU.mult,
                                           ALU.mult).then_inc(out_ready, 1)


def build(nc, a, out):
    z = Sizes(a["x"], a["w_in"], a["w_conv"], a["g_attn_out"], a["b_f"], a["w_up"], a["w_down"])
    with ExitStack() as ctx:
        m = Memory(nc, ctx)
        k = {
            "ident": m.sb("ident", [P, P]),
            "ident_bf": m.sb("ident_bf", [P, P], BF16),
            "causal": m.sb("causal", [P, P], BF16),
            "fold": m.sb("fold", [P, z.hd]),
            "eps": m.sb("eps", [P, 1]),
            "zero": m.sb("zero", [P, 1]),
            "rstd_conv": m.sb("rstd_conv", [P, z.tiles]),
            "rstd_attn": m.sb("rstd_attn", [P, z.tiles]),
            "w_ffn_conv": m.sb("w_ffn_conv_sb", [P, z.taps, 2 * z.ff // P]),
        }
        d = {
            "mix": nc.dram_tensor("mix", (z.conv + z.attn, z.seq), F32, kind="Internal").ap(),
            "qkv": nc.dram_tensor("qkv", (3, z.attn, z.seq), F32, kind="Internal").ap(),
            "gate_rows": nc.dram_tensor("gate_rows", (4, z.heads, z.seq), F32, kind="Internal").ap(),
            "x1": nc.dram_tensor("x1", (z.seq, z.d), F32, kind="Internal").ap(),
            "h2T": nc.dram_tensor("h2T", (z.d, z.seq), F32, kind="Internal").ap(),
        }
        project_inputs(nc, z, k, a, d)
        attend(nc, z, k, d)
        project_mix(nc, z, k, a, d)
        feed_forward(nc, z, k, a, d, out)


_INS = ["x", "g_mix", "w_in", "b_f", "w_conv", "g_conv_out", "g_attn_out", "w_o", "g_ffn", "w_up", "w_ffn_conv",
        "w_down", "g_final"]


def kernel(**inputs):
    import numpy as np
    from concourse import bacc
    from concourse.bass_utils import run_bass_kernel_spmd

    nc = bacc.Bacc("TRN2", target_bir_lowering=False, num_devices=1)
    arrays, args = {}, {}
    for name in _INS:
        array = np.ascontiguousarray(inputs[name])
        arrays[f"in_{name}"] = array
        args[name] = nc.dram_tensor(f"in_{name}", array.shape, mybir.dt.from_np(array.dtype), kind="ExternalInput").ap()
    out = nc.dram_tensor("out", inputs["x"].shape, F32, kind="ExternalOutput").ap()
    build(nc, args, out)
    r = run_bass_kernel_spmd(nc, [arrays], core_ids=[0])
    return r.results[0]["out"]
```
